# Optimizing a Trainium2 kernel written in Bass

```python
import jax, jax.numpy as jnp
from jax import lax
import numpy as np

D_MODEL = 2048
BATCH = 1
SEQ = 256
DEPTH = 1

N_MIXERS = 2
EPS = 1e-6
ML_HEADS = 8
ML_DQK = 128
ML_DV = 256
ML_CHUNK = 64
GATE_CAP = 15.0
SW_HEADS = 32
SW_KV_HEADS = 4
SW_HEAD_DIM = 64
SW_WINDOW = 128
SW_BLOCK = 128
D_FF = 5632
CONV_WIDTH = 3

kernel_name = "hybrid_mlstm_swa_convffn_adaln"

def rms_norm(x, eps=EPS):
    xf = x.astype(jnp.float32)
    return (xf * lax.rsqrt(jnp.mean(xf * xf, axis=-1, keepdims=True) + eps)).astype(x.dtype)

def modulation(c, w_mod, b_mod):
    m = jax.nn.silu(c) @ w_mod + b_mod
    return jnp.split(m[:, None, :], 6, axis=-1)

def mlstm_mixer(h, w_in, gate_bias, h_norm, w_out):
    B, S, _ = h.shape
    H, dk, dv, L = ML_HEADS, ML_DQK, ML_DV, ML_CHUNK
    f32 = jnp.float32
    proj = h @ w_in
    q, k, v, o, g = jnp.split(proj, [H * dk, 2 * H * dk, 2 * H * dk + H * dv, 2 * H * dk + 2 * H * dv], axis=-1)
    g = g.astype(f32) + gate_bias.astype(f32)
    g = GATE_CAP * jnp.tanh(g / GATE_CAP)
    i_pre = g[..., :H]
    log_f = jax.nn.log_sigmoid(g[..., H:])
    q = q.reshape(B, S, H, dk).astype(f32)
    k = k.reshape(B, S, H, dk).astype(f32) * (dk ** -0.5)
    v = v.reshape(B, S, H, dv).astype(f32)
    NC = S // L

    def chunks(t):
        t = t.reshape(B, NC, L, H, *t.shape[3:])
        return jnp.moveaxis(t, (1, 3), (0, 2))

    causal = jnp.tril(jnp.ones((L, L), dtype=bool))

    def step(carry, xs):
        C, n, m = carry
        qc, kc, vc, ic, fc = xs
        b = jnp.cumsum(fc, axis=-1)
        dmat = jnp.where(causal, b[..., :, None] - b[..., None, :] + ic[..., None, :], -jnp.inf)
        m_inter = b + m[..., None]
        m_t = jnp.maximum(m_inter, jnp.max(dmat, axis=-1))
        w_inter = jnp.exp(m_inter - m_t)
        p = jnp.exp(dmat - m_t[..., None]) * jnp.einsum('bhtd,bhsd->bhts', qc, kc)
        num = w_inter[..., None] * jnp.einsum('bhtd,bhdv->bhtv', qc, C) + jnp.einsum('bhts,bhsv->bhtv', p, vc)
        den = w_inter * jnp.einsum('bhtd,bhd->bht', qc, n) + jnp.sum(p, axis=-1)
        h_c = num / jnp.maximum(jnp.abs(den), jnp.exp(-m_t))[..., None]
        total = b[..., -1]
        g_s = total[..., None] - b + ic
        m_new = jnp.maximum(total + m, jnp.max(g_s, axis=-1))
        w_s = jnp.exp(g_s - m_new[..., None])
        decay = jnp.exp(total + m - m_new)
        C_new = decay[..., None, None] * C + jnp.einsum('bhs,bhsd,bhsv->bhdv', w_s, kc, vc)
        n_new = decay[..., None] * n + jnp.einsum('bhs,bhsd->bhd', w_s, kc)
        return (C_new, n_new, m_new), h_c

    init = (jnp.zeros((B, H, dk, dv), f32), jnp.zeros((B, H, dk), f32), jnp.zeros((B, H), f32))
    _, hs = lax.scan(step, init, (chunks(q), chunks(k), chunks(v), chunks(i_pre), chunks(log_f)))
    hs = jnp.moveaxis(hs, (0, 2), (1, 3)).reshape(B, S, H, dv)
    hs = rms_norm(hs) * h_norm.astype(f32).reshape(H, dv)
    out = jax.nn.sigmoid(o.astype(f32)) * hs.reshape(B, S, H * dv)
    return out.astype(h.dtype) @ w_out

def swa_mixer(h, w_qkv, q_norm, k_norm, sinks, w_out):
    B, S, _ = h.shape
    Hq, Hk, hd, BLK = SW_HEADS, SW_KV_HEADS, SW_HEAD_DIM, SW_BLOCK
    G = Hq // Hk
    f32 = jnp.float32
    qkv = h @ w_qkv
    q, k, v = jnp.split(qkv, [Hq * hd, Hq * hd + Hk * hd], axis=-1)
    q = rms_norm(q.reshape(B, S, Hk, G, hd)) * q_norm
    k = rms_norm(k.reshape(B, S, Hk, hd)) * k_norm
    v = v.reshape(B, S, Hk, hd)
    NB = S // BLK
    q_blocks = q.reshape(B, NB, BLK, Hk, G, hd).swapaxes(0, 1)

    def band(t):
        tp = jnp.pad(t, ((0, 0), (BLK, 0), (0, 0), (0, 0)))
        tb = tp.reshape(B, NB + 1, BLK, Hk, hd)
        return jnp.concatenate([tb[:, :-1], tb[:, 1:]], axis=2).swapaxes(0, 1)

    r = jnp.arange(2 * BLK)
    i = jnp.arange(BLK)
    rel = BLK + i[:, None] - r[None, :]
    band_mask = (rel >= 0) & (rel < SW_WINDOW)
    scale = hd ** -0.5
    sink_logits = sinks.astype(f32).reshape(Hk, G)[None, :, :, None, None]

    def block_attn(args):
        j, qb, kb, vb = args
        valid = band_mask & (r[None, :] + j * BLK >= BLK)
        s = jnp.einsum('bikgd,brkd->bkgir', qb.astype(f32), kb.astype(f32)) * scale
        s = jnp.where(valid, s, -jnp.inf)
        sink = jnp.broadcast_to(sink_logits, s.shape[:-1] + (1,))
        p = jax.nn.softmax(jnp.concatenate([s, sink], axis=-1), axis=-1)[..., :-1]
        return jnp.einsum('bkgir,brkd->bikgd', p, vb.astype(f32)).astype(qb.dtype)

    out = lax.map(block_attn, (jnp.arange(NB), q_blocks, band(k), band(v)))
    out = out.swapaxes(0, 1).reshape(B, S, Hq * hd)
    return out @ w_out

def conv_ffn(h, w_up, conv_w, conv_b, w_down):
    S = h.shape[1]
    u = h @ w_up
    up = jnp.pad(u, ((0, 0), (CONV_WIDTH - 1, 0), (0, 0)))
    u = sum(up[:, j:j + S] * conv_w[j] for j in range(CONV_WIDTH)) + conv_b
    gate, val = jnp.split(u, 2, axis=-1)
    return (jax.nn.silu(gate) * val) @ w_down

def setup_inputs(seed: int = 0) -> dict:
    key = jax.random.key(seed)
    ks = jax.random.split(key, 24)
    D, F = D_MODEL, D_FF
    H = ML_HEADS
    ml_in = 2 * H * ML_DQK + 2 * H * ML_DV + 2 * H
    sw_in = (SW_HEADS + 2 * SW_KV_HEADS) * SW_HEAD_DIM

    def nrm(k, shape, scale):
        return jax.random.normal(k, shape, jnp.float32) * scale

    f_bias = jnp.linspace(3.0, 6.0, H, dtype=jnp.float32)
    gate_bias = jnp.concatenate([nrm(ks[4], (H,), 0.1), f_bias + nrm(ks[5], (H,), 0.1)])
    return {
        "x": nrm(ks[0], (BATCH, SEQ, D), 1.0),
        "c": nrm(ks[1], (BATCH, D), 1.0),
        "l0_w_mod": nrm(ks[2], (D, 6 * D), 0.5 * D ** -0.5),
        "l0_b_mod": nrm(ks[3], (6 * D,), 0.01),
        "l0_w_in": nrm(ks[6], (D, ml_in), D ** -0.5),
        "l0_gate_bias": gate_bias,
        "l0_h_norm": 1.0 + nrm(ks[7], (H * ML_DV,), 0.02),
        "l0_w_out": nrm(ks[8], (H * ML_DV, D), (H * ML_DV) ** -0.5),
        "l0_w_up": nrm(ks[9], (D, 2 * F), D ** -0.5),
        "l0_conv_w": nrm(ks[10], (CONV_WIDTH, 2 * F), CONV_WIDTH ** -0.5),
        "l0_conv_b": nrm(ks[11], (2 * F,), 0.01),
        "l0_w_down": nrm(ks[12], (F, D), F ** -0.5),
        "l1_w_mod": nrm(ks[13], (D, 6 * D), 0.5 * D ** -0.5),
        "l1_b_mod": nrm(ks[14], (6 * D,), 0.01),
        "l1_w_qkv": nrm(ks[15], (D, sw_in), D ** -0.5),
        "l1_q_norm": 1.0 + nrm(ks[16], (SW_HEAD_DIM,), 0.02),
        "l1_k_norm": 1.0 + nrm(ks[17], (SW_HEAD_DIM,), 0.02),
        "l1_sinks": nrm(ks[18], (SW_HEADS,), 1.0),
        "l1_w_out": nrm(ks[19], (SW_HEADS * SW_HEAD_DIM, D), (SW_HEADS * SW_HEAD_DIM) ** -0.5),
        "l1_w_up": nrm(ks[20], (D, 2 * F), D ** -0.5),
        "l1_conv_w": nrm(ks[21], (CONV_WIDTH, 2 * F), CONV_WIDTH ** -0.5),
        "l1_conv_b": nrm(ks[22], (2 * F,), 0.01),
        "l1_w_down": nrm(ks[23], (F, D), F ** -0.5),
    }

def reference(x, c, l0_w_mod, l0_b_mod, l0_w_in, l0_gate_bias, l0_h_norm, l0_w_out, l0_w_up, l0_conv_w, l0_conv_b, l0_w_down, l1_w_mod, l1_b_mod, l1_w_qkv, l1_q_norm, l1_k_norm, l1_sinks, l1_w_out, l1_w_up, l1_conv_w, l1_conv_b, l1_w_down):
    mod_params = [(l0_w_mod, l0_b_mod), (l1_w_mod, l1_b_mod)]
    ffn_params = [(l0_w_up, l0_conv_w, l0_conv_b, l0_w_down), (l1_w_up, l1_conv_w, l1_conv_b, l1_w_down)]
    for layer in range(DEPTH):
        sh1, sc1, g1, sh2, sc2, g2 = modulation(c, *mod_params[layer])
        hm = rms_norm(x) * (1.0 + sc1) + sh1
        if layer % N_MIXERS == 0:
            y = mlstm_mixer(hm, l0_w_in, l0_gate_bias, l0_h_norm, l0_w_out)
        else:
            y = swa_mixer(hm, l1_w_qkv, l1_q_norm, l1_k_norm, l1_sinks, l1_w_out)
        x = x + g1 * y
        hf = rms_norm(x) * (1.0 + sc2) + sh2
        x = x + g2 * conv_ffn(hf, *ffn_params[layer])
    return x


_drawn_inputs = setup_inputs


def setup_inputs(seed=0):
    import zlib

    import numpy as np

    out = dict(_drawn_inputs(seed))
    spreads = {}
    factors = {'l0_b_mod': 4.938, 'l0_h_norm': 78.974, 'l0_conv_b': 87.613}
    for name, (base, spread) in spreads.items():
        noise = np.random.default_rng([zlib.crc32(name.encode()), seed]).standard_normal(out[name].shape)
        drawn = base * np.exp(spread * noise) if base else spread * noise
        out[name] = __import__('jax').numpy.asarray(drawn.astype(out[name].dtype))
    for name, factor in factors.items():
        out[name] = (out[name] * factor).astype(out[name].dtype)
    return out
```

```python
import concourse.bass as bass
from concourse import mybir
from contextlib import ExitStack


def hybrid_mlstm_convffn_adaln_kernel(nc, x_d, c_d, w_mod, b_mod, w_in, gate_bias, h_norm, w_out,
                                      w_up, conv_w, conv_b, w_down, out_d):
    f32 = mybir.dt.float32
    f32r = mybir.dt.float32r
    ALU = mybir.AluOpType
    ACT = mybir.ActivationFunctionType
    ds = bass.ds

    P = 128
    SEQ, D = x_d.shape[1], x_d.shape[2]
    TB = SEQ // P
    KT = D // P
    H = gate_bias.shape[0] // 2
    DV = h_norm.shape[0] // H
    DK = (w_in.shape[1] - 2 * H * DV - 2 * H) // (2 * H)
    F = w_down.shape[0]
    FT = F // P
    COL_K, COL_V, COL_O, COL_G = H * DK, 2 * H * DK, 2 * H * DK + H * DV, 2 * H * DK + 2 * H * DV
    EPS, GATE_CAP = 1e-6, 15.0
    QUARTER = 512
    UNIT = D
    HALF = UNIT // 2
    MASKED = 1e4
    assert (TB, KT, DK, DV, H) == (2, 16, 128, 256, 8) and FT == 44

    U_V, U_HEAD, U_OUT = 0, 16, 48
    CHUNKS = [16, 16, 12]
    U_UP, U_DOWN, u = [], [], U_OUT + 16
    for n in CHUNKS:
        U_UP.append(u)
        U_DOWN.append(u + 2 * n)
        u += 3 * n
    N_UNITS = u
    F_TILE = [0, 16, 32]
    MODS_ALONE = 2 * KT
    A_HEAD = 0
    A_UP, a = [], 4 * H
    for n, k in enumerate(CHUNKS):
        A_UP.append(a)
        a += 2 * k + (4 if n == 0 else 0)
    A_G2 = A_UP[0] + 2 * CHUNKS[0]
    PAIR0 = F_TILE
    Y_OUT, Y_DOWN = 0, [4, 8, 12]
    C_SH1, C_SC1, C_G1, C_SH2, C_SC2, C_G2 = (D * n for n in range(6))
    MOD_ORDER = [C_SC1, C_SH1, C_G1, C_SC2, C_SH2, C_G2]

    with ExitStack() as ctx:
        def sem(name):
            return ctx.enter_context(nc.semaphore(name))

        KB = 1024
        BASE = (nc.sbuf_base + 63) // 64 * 64

        def place(name, shape, offset, dt=f32):
            return nc.alloc_sbuf_tensor_at(name, shape, dt, offset=BASE + offset)

        raw = place("raw", [P, 4, UNIT], 0)
        w_hi = place("w_hi", [P, 4, HALF], 32 * KB, f32r)
        w_lo = place("w_lo", [P, 4, HALF], 48 * KB, f32r)
        mod_raw = place("mod_raw", [P, 2, UNIT], 64 * KB)
        acc = place("acc", [P, 2, D], 80 * KB)
        g_bc = place("g_bc", [P, D], 96 * KB)
        x = place("x", [P, TB, D], 104 * KB)
        hm_hi = place("hm_hi", [P, KT, SEQ], 120 * KB, f32r)
        hm_lo = place("hm_lo", [P, KT, SEQ], 136 * KB, f32r)
        v = place("v", [P, TB, H * DV], 152 * KB)
        o_hi = place("o_hi", [P, KT * SEQ], 168 * KB, f32r)
        o_lo = place("o_lo", [P, KT * SEQ], 184 * KB, f32r)
        tail = 200 * KB
        xn = place("xn", [P, TB, D], 168 * KB)
        xnT = place("xnT", [P, KT, SEQ], 184 * KB)
        act_hi = place("act_hi", [P, 16 * SEQ], 152 * KB, f32r)
        act_lo = place("act_lo", [P, 16 * SEQ], 168 * KB, f32r)
        c_rows = place("c_rows", [KT, P], 96 * KB)
        hn_rows = place("hn_rows", [KT, P], 96 * KB + 512)
        cv_rows = place("cv_rows", [2 * FT, 4, P], 97 * KB)
        wg_raw = place("wg_raw", [P, KT * 2 * H], 168 * KB)
        wg_hi = place("wg_hi", [P, KT, 2 * H], 169 * KB, f32r)
        wg_lo = place("wg_lo", [P, KT, 2 * H], 170 * KB, f32r)
        g_sb = place("g_sb", [P, TB, 2 * H], 171 * KB)
        th_i = place("th_i", [H, SEQ], 172 * KB)
        th_f = place("th_f", [H, SEQ], 173 * KB)
        exp_f = place("exp_f", [H, SEQ], 174 * KB)
        neg_lf = place("neg_lf", [H, SEQ], 175 * KB)
        neg_b = place("neg_b", [H, SEQ], 176 * KB)
        a_row = place("a_row", [H, SEQ], 177 * KB)
        neg_m = place("neg_m", [H, SEQ], 178 * KB)
        em_row = place("em_row", [H, SEQ], 179 * KB)
        ones_row = place("ones_row", [H, SEQ], 180 * KB)
        kT = place("kT", [P, SEQ], 80 * KB)
        qT = place("qT", [P, SEQ], 81 * KB)
        weights = place("weights", [P, 384], 82 * KB)
        probs = place("probs", [P, 384], 82 * KB + 1536)
        m_row = place("m_row", [H, SEQ], 85 * KB)
        m_sel = place("m_sel", [H, SEQ], 82 * KB)
        h_tok = place("h_tok", [P, TB, DV], 82 * KB)
        gated = place("gated", [P, 2 * SEQ], 86 * KB)
        conv_gate = place("conv_gate", [P, 2, SEQ], 80 * KB)
        conv_val = place("conv_val", [P, 2, SEQ], 82 * KB)
        act_full = place("act_full", [P, 2, SEQ], 84 * KB)

        ident = place("ident", [P, P], tail)
        ones = place("ones", [P, P], tail + 512)
        mask = place("mask", [P, SEQ], tail + KB)
        o_sig = place("o_sig", [P, 2 * SEQ], tail + 2 * KB)
        y_tmp = place("y_tmp", [P, TB, QUARTER], tail + 2 * KB)
        cT = place("cT", [P, KT], tail + 6144)
        hnT = place("hnT", [P, KT], tail + 6208)
        cvT = place("cvT", [P, 4 * 2 * FT], tail + 6272)
        scale_p = place("scale_p", [P, KT], tail + 7680)
        shift_p = place("shift_p", [P, KT], tail + 7744)
        a_em = place("a_em", [P, 4, H], tail + 7808)
        small = place("small", [P, 13, TB], tail + 7936)
        (ss, ms, rstd, neg_den, den_abs, den_max, rden, h_ss, h_ms, h_rstd, minus_half) = (
            small[:, n, :] for n in range(11))
        gate_b, gate_b15 = small[0:H, 11, :], small[0:H, 12, :]

        ps = ctx.enter_context(nc.psum_tensor("ps", [P, 8, 512], f32))

        c_in, hn_in, cv_in, gb_in = sem("c_in"), sem("hn_in"), sem("cv_in"), sem("gb_in")
        sp_began, pool_began = sem("sp_began"), sem("pool_began")
        x_in = [sem(f"x_in{t}") for t in range(TB)]
        wg_in = sem("wg_in")
        consts_made = sem("consts_made")
        pool_step = sem("pool_step")
        raw_in = [sem(f"raw_in{s}") for s in range(4)]
        raw_done = sem("raw_done")
        w_hi_made = sem("w_hi_made")
        half_done = sem("half_done")
        mod_in = [sem(f"mod_in{s}") for s in range(2)]
        mod_done = sem("mod_done")
        acc_cleared = sem("acc_cleared")
        acc_first = [sem(f"acc_first{s}") for s in range(2)]
        acc_ready = [sem(f"acc_ready{s}") for s in range(2)]
        colsum_done = sem("colsum_done")
        silu_c = sem("silu_c")
        params_T = sem("params_T")
        params_made = sem("params_made")
        sc_made = sem("sc_made")
        sq_made = sem("sq_made")
        ms_made = sem("ms_made")
        rstd_made = sem("rstd_made")
        xn_made = sem("xn_made")
        xT_ready = sem("xT_ready")
        xT_copied = sem("xT_copied")
        hm_hi_made, hm_full, hm_made = sem("hm_hi_made"), sem("hm_full"), sem("hm_made")
        v_copied = sem("v_copied")
        wg_hi_made, wg_made = sem("wg_hi_made"), sem("wg_made")
        g_ready, g_copied, g_rows = sem("g_ready"), sem("g_copied"), sem("g_rows")
        gb_scaled = sem("gb_scaled")
        th_made, ef_made, lf_made = sem("th_made"), sem("ef_made"), sem("lf_made")
        b_made, a_made, m_made, nm_made, em_made = (sem("b_made"), sem("a_made"), sem("m_made"),
                                                    sem("nm_made"), sem("em_made"))
        aem_ready, aem_made = sem("aem_ready"), sem("aem_made")
        g_summed, g_bc_made = sem("g_summed"), sem("g_bc_made")
        a_free = sem("a_free")
        m_sel_made = sem("m_sel_made")
        scores_made = sem("scores_made")
        gaps_made = sem("gaps_made")
        exp_made, probs_made, pv_done = sem("exp_made"), sem("probs_made"), sem("pv_done")
        den_step, rden_made = sem("den_step"), sem("rden_made")
        h_ss_made, h_ms_made, h_rstd_made = sem("h_ss_made"), sem("h_ms_made"), sem("h_rstd_made")
        h_made, hT_ready, sig_made = sem("h_made"), sem("hT_ready"), sem("sig_made")
        gated_made, o_hi_made, o_made = sem("gated_made"), sem("o_hi_made"), sem("o_made")
        y_scaled = sem("y_scaled")
        x_added = sem("x_added")
        conv_base, tap1_made = sem("conv_base"), sem("tap1_made")
        silu_made, act_hi_made, prod_made = sem("silu_made"), sem("act_hi_made"), sem("prod_made")
        pair_done = sem("pair_done")
        out_stored = sem("out_stored")

        RAW0 = 8 + 2 * MODS_ALONE

        def mod_rows(t):
            return ds(t * P, P)

        def a_src(w, col):
            return w[:, ds(col, P)].rearrange("(k p) n -> p k n", p=P)

        def b_src(w, row, col):
            return w[ds(row, 4 * P), ds(col, QUARTER)].rearrange("(k p) n -> p k n", p=P)

        block = ctx.enter_context(nc.Block())

        @block.sync
        def _(sp):
            def load(use, src, shape_k, plus=0):
                sp.wait_ge(raw_done, plus * 2 + 2 * use + 2)
                sp.sem_inc(sp_began, 1)
                dst = raw[:, use % 4, :].rearrange("p (k n) -> p k n", k=shape_k)
                sp.dma_start(dst, src).then_inc(raw_in[use % 4], 16)

            def load_mod(m, tile, col, plus=0):
                sp.wait_ge(mod_done, plus + m - MODS_ALONE + 1)
                sp.sem_inc(sp_began, 1)
                sp.dma_start(mod_raw[:, m % 2, :], w_mod[mod_rows(tile), col:col + D])\
                  .then_inc(mod_in[m % 2], 16)

            def load_v(quarter, r, plus=0):
                load(W0 + U_V + r, b_src(w_in, 4 * P * r, COL_V + QUARTER * quarter), 4, plus)

            def load_head(h, r, plus=0):
                col = (COL_K + DK * h, DK * h, COL_O + DV * h, COL_O + DV * h + P)[r]
                load(W0 + U_HEAD + r, a_src(w_in, col), KT, plus)

            def load_out(quarter, r, plus=0):
                load(W0 + U_OUT + r, b_src(w_out, 4 * P * r, QUARTER * quarter), 4, plus)

            def load_up(n, i, r, plus=0):
                col = 2 * P * i + P * (F_TILE[n] + r // 2) + (F if r % 2 else 0)
                load(W0 + U_UP[n] + r, a_src(w_up, col), KT, plus)

            def load_down(n, quarter, r, plus=0):
                load(W0 + U_DOWN[n] + r, b_src(w_down, P * F_TILE[n] + 4 * P * r, QUARTER * quarter),
                     4, plus)

            W0 = MODS_ALONE
            sp.dma_start(c_rows[:], c_d[0, :].rearrange("(k p) -> k p", p=P)).then_inc(c_in, 16)
            for n in range(2):
                sp.wait_ge(acc_cleared, n + 1)
                sp.dma_start(acc[0:1, n, :], b_mod[MOD_ORDER[n]:MOD_ORDER[n] + D]
                             .rearrange("(a n) -> a n", a=1)).then_inc(acc_first[n], 16)
                with sp.Fori(0, KT // 4) as i:
                    for r in range(4):
                        load(KT * n + r, w_mod[mod_rows(4 * i + r), MOD_ORDER[n]:MOD_ORDER[n] + D],
                             1, plus=4 * i)
                if n == 0:
                    for t in range(TB):
                        sp.dma_start(x[:, t, :], x_d[0, t * P:(t + 1) * P, :]).then_inc(x_in[t], 16)
            for r in range(4):
                load_v(0, r)
            with sp.Fori(0, 3) as i:
                for r in range(4):
                    load_mod(2 * KT + r, 4 * i + r, C_G1, plus=4 * i)
                    load(W0 + U_V + 4 + r, b_src(w_in, 4 * P * r, COL_V + QUARTER * (i + 1)), 4,
                         plus=4 * i)
            for r in range(4):
                load_mod(3 * KT - 4 + r, KT - 4 + r, C_G1)
                load_head(0, r)
            with sp.Fori(0, H - 1) as h:
                for r in range(4):
                    if r % 2 == 0:
                        load_mod(3 * KT + r // 2, 2 * h + r // 2, C_SC2, plus=2 * h)
                    load(W0 + U_HEAD + 4 + r, a_src(w_in, (COL_K + DK * (h + 1), DK * (h + 1),
                                                           COL_O + DV * (h + 1),
                                                           COL_O + DV * (h + 1) + P)[r]),
                         KT, plus=4 * h)
            for r in range(4):
                if r % 2 == 0:
                    load_mod(4 * KT - 2 + r // 2, KT - 2 + r // 2, C_SC2)
                load_out(0, r)
            with sp.Fori(0, 3) as i:
                for r in range(4):
                    load_mod(4 * KT + r, 4 * i + r, C_SH2, plus=4 * i)
                    load(W0 + U_OUT + 4 + r, b_src(w_out, 4 * P * r, QUARTER * (i + 1)), 4,
                         plus=4 * i)
            for r in range(4):
                load_mod(5 * KT - 4 + r, KT - 4 + r, C_SH2)
                load_up(0, 0, r)
            with sp.Fori(0, KT // 2 - 1) as i:
                for r in range(4):
                    if r % 2 == 0:
                        load_mod(5 * KT + r // 2, 2 * i + r // 2, C_G2, plus=2 * i)
                    load(W0 + U_UP[0] + 4 + r,
                         a_src(w_up, 2 * P * (i + 1) + P * (r // 2) + (F if r % 2 else 0)), KT,
                         plus=4 * i)
            for r in range(4):
                if r % 2 == 0:
                    load_mod(6 * KT - 2 + r // 2, KT - 2 + r // 2, C_G2)
                load_down(0, 0, r)
            for n, tiles in enumerate(CHUNKS):
                if n:
                    with sp.Fori(0, tiles // 2) as i:
                        for r in range(4):
                            load_up(n, i, r, 4 * i)
                if n == 0:
                    with sp.Fori(0, 3) as i:
                        for r in range(4):
                            load(W0 + U_DOWN[0] + 4 + r,
                                 b_src(w_down, 4 * P * r, QUARTER * (i + 1)), 4, plus=4 * i)
                elif tiles == 16:
                    with sp.Fori(0, 4) as i:
                        for r in range(4):
                            load_down(n, i, r, 4 * i)
                else:
                    for q in range(4):
                        for r in range(tiles // 4):
                            load(W0 + U_DOWN[n] + q * (tiles // 4) + r,
                                 b_src(w_down, P * F_TILE[n] + 4 * P * r, QUARTER * q), 4)
            for q in range(4):
                for t in range(TB):
                    sp.wait_ge(x_added, 2 + 2 * (Y_DOWN[-1] + q) + t + 1)
                    sp.dma_start(out_d[0, t * P:(t + 1) * P, q * QUARTER:(q + 1) * QUARTER],
                                 x[:, t, q * QUARTER:(q + 1) * QUARTER]).then_inc(out_stored, 16)
            sp.wait_ge(out_stored, 16 * 4 * TB)

        @block.gpsimd
        def _(pool):
            pool.sem_inc(raw_done, 8)
            pool.sem_inc(mod_done, 2)
            pool.sem_inc(v_copied, 4)
            pool.sem_inc(y_scaled, 4)
            pool.sem_inc(x_added, 2)
            pool.sem_inc(pair_done, 2)
            for free, count in ((scores_made, 1), (probs_made, 1), (pv_done, 1), (h_made, 2),
                                (gated_made, 2), (o_made, 1)):
                pool.sem_inc(free, count)
            nc.gpsimd.memset(ident[:], 0.0).then_inc(pool_step, 1)
            nc.gpsimd.memset(mask[:], 0.0).then_inc(pool_step, 1)
            pool.wait_ge(pool_step, 2)
            nc.gpsimd.affine_select(out=ident[:], in_=ident[:], compare_op=ALU.not_equal, fill=1.0,
                                    base=0, pattern=[[-1, P]], channel_multiplier=1)\
                     .then_inc(consts_made, 1)
            nc.gpsimd.affine_select(out=mask[:, 0:P], in_=mask[:, 0:P], compare_op=ALU.is_ge,
                                    fill=MASKED, base=0, pattern=[[1, P]], channel_multiplier=-1)\
                     .then_inc(consts_made, 1)
            nc.gpsimd.memset(ones[:], 1.0).then_inc(consts_made, 1)
            nc.gpsimd.memset(minus_half, -0.5).then_inc(consts_made, 1)

            def clear_acc(n):
                pool.wait_ge(colsum_done, n - 1)
                nc.gpsimd.memset(acc[:, n % 2, :], 0.0).then_inc(acc_cleared, 1)
                pool.wait_ge(acc_cleared, n + 1)
                col = MOD_ORDER[n]
                pool.dma_start(acc[0:1, n % 2, :], b_mod[col:col + D].rearrange("(a n) -> a n", a=1))\
                    .then_inc(acc_ready[n % 2], 16)

            def rstd_of_x(n):
                pool.wait_ge(sq_made, TB * (n + 1))
                nc.gpsimd.tensor_scalar(ms, ss, 1.0 / D, EPS, ALU.mult, ALU.add)\
                         .then_inc(ms_made, 1)
                pool.wait_ge(ms_made, n + 1)
                nc.gpsimd.tensor_tensor(rstd, ms, minus_half, ALU.pow).then_inc(rstd_made, 1)

            rstd_of_x(0)
            pool.wait_ge(xT_ready, KT // 2)
            pool.dma_start(wg_raw[:].rearrange("p (k n) -> p k n", k=KT),
                           w_in[:, COL_G:COL_G + 2 * H].rearrange("(k p) n -> p k n", p=P))\
                .then_inc(wg_in, 16)
            nc.gpsimd.memset(ones_row[:], 1.0).then_inc(consts_made, 1)
            pool.wait_ge(wg_in, 16)
            wg_hi2 = wg_hi[:].rearrange("p k n -> p (k n)")
            nc.gpsimd.tensor_copy(wg_hi2, wg_raw[:]).then_inc(wg_hi_made, 1)
            pool.wait_ge(wg_hi_made, 1)
            nc.gpsimd.tensor_tensor(wg_lo[:].rearrange("p k n -> p (k n)"), wg_raw[:],
                                    wg_hi2.bitcast(f32), ALU.subtract).then_inc(wg_made, 1)
            clear_acc(2)
            clear_acc(3)

            def head(h):
                pool.wait_ge(a_free, 4 + A_HEAD + 4 * h + 4)
                pool.sem_inc(pool_began, 1)
                nc.gpsimd.tensor_scalar(o_sig[:], o_sig[:], 0.5, 0.5, ALU.mult, ALU.add)\
                         .then_inc(sig_made, 1)
                pool.wait_ge(h_ss_made, 2 * h + 2)
                pool.sem_inc(pool_began, 1)
                nc.gpsimd.tensor_scalar(h_ms, h_ss, 1.0 / DV, EPS, ALU.mult, ALU.add)\
                         .then_inc(h_ms_made, 1)
                pool.wait_ge(h_ms_made, h + 1)
                nc.gpsimd.tensor_tensor(h_rstd, h_ms, minus_half, ALU.pow)\
                         .then_inc(h_rstd_made, 1)
                pool.wait_ge(o_hi_made, h + 1)
                nc.gpsimd.tensor_tensor(o_lo[:, ds(2 * SEQ * h, 2 * SEQ)], gated[:],
                                        o_hi[:, ds(2 * SEQ * h, 2 * SEQ)].bitcast(f32),
                                        ALU.subtract).then_inc(o_made, 1)

            with pool.Fori(0, H) as h:
                head(h)
            pool.wait_ge(o_made, H + 1)
            clear_acc(4)

            def add_y(yq, i=0):
                for t in range(TB):
                    pool.wait_ge(y_scaled, 4 + 2 * (yq + i) + t + 1)
                    part = x[:, t, ds((yq % 4 + i) * QUARTER, QUARTER)]
                    nc.gpsimd.tensor_tensor(part, part, y_tmp[:, t, :], ALU.add).then_inc(x_added, 1)

            with pool.Fori(0, 4) as i:
                add_y(Y_OUT, i)
            rstd_of_x(1)
            clear_acc(5)
            for n, tiles in enumerate(CHUNKS):
                with pool.Fori(0, tiles // 2) as i:
                    for k in range(2):
                        pair = PAIR0[n] + k
                        unit = A_UP[n] + 2 * k + 1
                        part = ds((2 * i + k) * SEQ, SEQ)
                        pool.wait_ge(silu_made, 2 * i + pair + 1)
                        pool.wait_ge(a_free, 4 + 4 * i + unit + 1)
                        nc.gpsimd.tensor_tensor(act_full[:, k, :], conv_gate[:, k, :],
                                                conv_val[:, k, :], ALU.mult).then_inc(prod_made, 1)
                        pool.wait_ge(prod_made, 2 * i + pair + 1)
                        pool.wait_ge(act_hi_made, 2 * i + pair + 1)
                        nc.gpsimd.tensor_tensor(act_lo[:, part], act_full[:, k, :],
                                                act_hi[:, part].bitcast(f32), ALU.subtract)\
                                 .then_inc(pair_done, 1)
                with pool.Fori(0, 4) as i:
                    add_y(Y_DOWN[n], i)

        @block.scalar
        def _(act):
            def split_hi(v, plus=0):
                if v >= 2 * N_UNITS:
                    return
                if v % 2 == 0:
                    act.wait_ge(raw_in[v // 2 % 4], 16 * (MODS_ALONE // 4 + v // 8 + 1) + 2 * plus)
                nc.scalar.activation(w_hi[:, v % 4, :],
                                     raw[:, v // 2 % 4, (v % 2) * HALF:(v % 2 + 1) * HALF],
                                     ACT.Copy).then_inc(w_hi_made, 1)

            def first_half(u, plus=0):
                act.wait_ge(half_done, 2 * u + 1 + plus)
                split_hi(2 * u + 4, plus)

            def second_half(u, plus=0):
                act.wait_ge(half_done, 2 * u + 2 + plus)

            def sums_of_squares():
                for t in range(TB):
                    nc.scalar.activation(xn[:, t, :], x[:, t, :], ACT.Square,
                                         accum_out=ss[:, t:t + 1]).then_inc(sq_made, 1)

            def normalise(n):
                act.wait_ge(rstd_made, n + 1)
                for t in range(TB):
                    nc.scalar.activation(xn[:, t, :], x[:, t, :], ACT.Copy,
                                         scale=rstd[:, t:t + 1]).then_inc(xn_made, 1)

            def copy_xT(n):
                for g in range(KT // 2):
                    act.wait_ge(xT_ready, n * KT // 2 + g + 1)
                    nc.scalar.activation(xnT[:, 2 * g:2 * g + 2, :].rearrange("p k t -> p (k t)"),
                                         ps[:, 4 + g % 4, :], ACT.Copy).then_inc(xT_copied, 1)

            def modulate_hi(n, first, last):
                for k in range(first, last):
                    nc.scalar.activation(hm_hi[:, k, :], xnT[:, k, :], ACT.Identity,
                                         bias=shift_p[:, k:k + 1], scale=scale_p[:, k:k + 1])\
                             .then_inc(hm_hi_made, 1)

            nc.scalar.preload_act_table(ACT.Silu)
            act.dma_start(hn_rows[:], h_norm.rearrange("(k p) -> k p", p=P)).then_inc(hn_in, 16)
            act.dma_start(cv_rows[:, 0:3, :], conv_w.rearrange("j (f p) -> f j p", p=P))\
               .then_inc(cv_in, 16)
            act.dma_start(cv_rows[:, 3, :], conv_b.rearrange("(f p) -> f p", p=P)).then_inc(cv_in, 16)
            for j in range(2):
                act.dma_start(gate_b[:, j:j + 1], gate_bias[j * H:(j + 1) * H]
                              .rearrange("(h o) -> h o", o=1)).then_inc(gb_in, 16)
            act.wait_ge(c_in, 16)
            nc.scalar.activation(c_rows[:], c_rows[:], ACT.Silu).then_inc(silu_c, 1)
            act.wait_ge(params_T, 1)
            nc.scalar.activation(cT[:], ps[:, 0, 0:KT], ACT.Copy).then_inc(params_made, 1)
            for t in range(TB):
                act.wait_ge(x_in[t], 16)
            sums_of_squares()
            normalise(0)
            act.wait_ge(params_T, 2)
            nc.scalar.activation(hnT[:], ps[:, 1, 0:KT], ACT.Copy).then_inc(params_made, 1)
            act.wait_ge(params_T, 3)
            nc.scalar.activation(cvT[:], ps[:, 2, 0:4 * 2 * FT], ACT.Copy).then_inc(params_made, 1)
            copy_xT(0)

            def scale_shift(n, bank, out, plus_one):
                act.wait_ge(colsum_done, n + 1)
                if plus_one:
                    nc.scalar.activation(out[:], ps[:, bank, 0:KT], ACT.Copy, bias=1.0)\
                             .then_inc(sc_made, 1)
                else:
                    nc.scalar.activation(out[:], ps[:, bank, 0:KT], ACT.Copy).then_inc(sc_made, 1)

            scale_shift(0, 0, scale_p, True)
            scale_shift(1, 1, shift_p, False)
            act.wait_ge(sc_made, 2)
            for g in range(4):
                modulate_hi(0, 4 * g, 4 * g + 4)
                split_hi(g)
            with act.Fori(0, 2) as i:
                for r in range(8):
                    first_half(U_V + r, 16 * i)
                    second_half(U_V + r, 16 * i)
                    if r % 4 == 3:
                        for t in range(TB):
                            nc.scalar.activation(v[:, t, ds((2 * i + r // 4) * QUARTER, QUARTER)],
                                                 ps[:, 2 * (r // 4) + t, :], ACT.Copy)\
                                     .then_inc(v_copied, 1)
                    split_hi(2 * (U_V + r) + 5, 16 * i)
            act.wait_ge(g_ready, 1)
            nc.scalar.activation(g_sb[:].rearrange("p t n -> p (t n)"), ps[:, 0, 0:TB * 2 * H],
                                 ACT.Copy).then_inc(g_copied, 1)

            def copy_g_bc(n):
                for b in range(4):
                    act.wait_ge(g_summed, 4 * n + b + 1)
                    nc.scalar.activation(g_bc[:, b * QUARTER:(b + 1) * QUARTER], ps[:, 4 + b, :],
                                         ACT.Copy).then_inc(a_free, 1)

            copy_g_bc(0)
            first_half(U_HEAD)
            second_half(U_HEAD)
            nc.scalar.activation(kT[:], ps[:, 4, 0:SEQ], ACT.Copy).then_inc(a_free, 1)
            split_hi(2 * U_HEAD + 5)
            act.wait_ge(g_rows, 1)
            act.wait_ge(gb_scaled, 1)
            nc.scalar.activation(th_i[:], ps[0:H, 1, 0:SEQ], ACT.Tanh, bias=gate_b15[:, 0:1],
                                 scale=1.0 / GATE_CAP).then_inc(th_made, 1)
            nc.scalar.activation(th_f[:], ps[0:H, 1, SEQ:2 * SEQ], ACT.Tanh, bias=gate_b15[:, 1:2],
                                 scale=1.0 / GATE_CAP).then_inc(th_made, 1)
            act.wait_ge(th_made, 2)
            nc.scalar.activation(exp_f[:], th_f[:], ACT.Exp, scale=-GATE_CAP).then_inc(ef_made, 1)
            act.wait_ge(ef_made, 1)
            nc.scalar.activation(neg_lf[:], exp_f[:], ACT.Ln, bias=ones_row[:, 0:1])\
                     .then_inc(lf_made, 1)
            first_half(U_HEAD + 1)
            second_half(U_HEAD + 1)
            nc.scalar.activation(qT[:], ps[:, 5, 0:SEQ], ACT.Copy).then_inc(a_free, 1)
            split_hi(2 * U_HEAD + 7)
            act.wait_ge(nm_made, 1)
            nc.scalar.activation(em_row[:], neg_m[:], ACT.Exp).then_inc(em_made, 1)
            act.wait_ge(aem_ready, 1)
            nc.scalar.activation(a_em[:].rearrange("p a h -> p (a h)"), ps[:, 0, 0:4 * H], ACT.Copy)\
                     .then_inc(aem_made, 1)

            def head(h, last):
                if last:
                    h, u, a, plus = H - 1, U_HEAD + 2 + 4 * (H - 1), 0, 0
                else:
                    u, plus = U_HEAD + 2, 8 * h
                first_half(u, plus)
                second_half(u, plus)
                act.wait_ge(gated_made, 2 * h + 2)
                nc.scalar.activation(o_sig[:, 0:SEQ], ps[:, 6, 0:SEQ], ACT.Tanh, scale=0.5)\
                         .then_inc(a_free, 1)
                split_hi(2 * u + 5, plus)
                act.wait_ge(gaps_made, 2 * h + 2)
                nc.scalar.activation(weights[:], weights[:], ACT.Exp, scale=-1.0).then_inc(exp_made, 1)
                first_half(u + 1, plus)
                second_half(u + 1, plus)
                nc.scalar.activation(o_sig[:, SEQ:2 * SEQ], ps[:, 7, 0:SEQ], ACT.Tanh, scale=0.5)\
                         .then_inc(a_free, 1)
                split_hi(2 * u + 7, plus)
                act.wait_ge(rden_made, h + 1)
                act.wait_ge(h_made, 2 * h + 2)
                for t in range(TB):
                    nc.scalar.activation(h_tok[:, t, :], ps[:, 2 + t, 0:DV], ACT.Square,
                                         scale=rden[:, t:t + 1], accum_out=h_ss[:, t:t + 1])\
                             .then_inc(h_ss_made, 1)
                if not last:
                    first_half(u + 2, plus)
                    second_half(u + 2, plus)
                    nc.scalar.activation(kT[:], ps[:, 4, 0:SEQ], ACT.Copy).then_inc(a_free, 1)
                    split_hi(2 * u + 9, plus)
                    first_half(u + 3, plus)
                act.wait_ge(gated_made, 2 * h + 4)
                nc.scalar.activation(o_hi[:, ds(2 * SEQ * h, 2 * SEQ)], gated[:], ACT.Copy)\
                         .then_inc(o_hi_made, 1)
                if not last:
                    second_half(u + 3, plus)
                    nc.scalar.activation(qT[:], ps[:, 5, 0:SEQ], ACT.Copy).then_inc(a_free, 1)
                    split_hi(2 * u + 11, plus)

            nc.scalar.preload_act_table_set("exp_and_others")
            with act.Fori(0, H - 1) as h:
                head(h, False)
            head(H - 1, True)
            scale_shift(3, 1, scale_p, True)
            nc.scalar.preload_act_table_set("silu_and_others")
            with act.Fori(0, 2) as i:
                for r in range(8):
                    first_half(U_OUT + r, 16 * i)
                    second_half(U_OUT + r, 16 * i)
                    split_hi(2 * (U_OUT + r) + 5, 16 * i)
            act.wait_ge(x_added, 2 + 2 * 4)
            sums_of_squares()
            normalise(1)
            copy_xT(1)
            scale_shift(4, 0, shift_p, False)
            act.wait_ge(sc_made, 4)
            modulate_hi(1, 0, KT)
            for n, tiles in enumerate(CHUNKS):
                with act.Fori(0, tiles // 2) as i:
                    for r in range(4):
                        u, pair = U_UP[n] + r, PAIR0[n] + r // 2
                        a = A_UP[n] + r
                        dst = (conv_val if r % 2 else conv_gate)[:, r // 2, :]
                        col = 2 * i + (FT if r % 2 else 0) + pair
                        first_half(u, 8 * i)
                        if r % 2:
                            act.wait_ge(a_free, 4 * i + 4 + a)
                            nc.scalar.activation(conv_gate[:, r // 2, :], conv_gate[:, r // 2, :],
                                                 ACT.Silu).then_inc(silu_made, 1)
                        second_half(u, 8 * i)
                        act.wait_ge(pair_done, 2 * i + pair + 1)
                        nc.scalar.activation(dst, ps[:, 4 + r, 0:SEQ], ACT.Identity,
                                             bias=cvT[:, ds(col + 3 * 2 * FT, 1)],
                                             scale=cvT[:, ds(col + 2 * 2 * FT, 1)])\
                                 .then_inc(conv_base, 1)
                        split_hi(2 * u + 5, 8 * i)
                if n == 0:
                    copy_g_bc(1)
                if tiles == 16:
                    with act.Fori(0, 2) as i:
                        for r in range(8):
                            first_half(U_DOWN[n] + r, 16 * i)
                            second_half(U_DOWN[n] + r, 16 * i)
                            split_hi(2 * (U_DOWN[n] + r) + 5, 16 * i)
                else:
                    for r in range(tiles):
                        if 2 * (U_DOWN[n] + r) + 4 < 2 * N_UNITS:
                            first_half(U_DOWN[n] + r)
                            second_half(U_DOWN[n] + r)
                            split_hi(2 * (U_DOWN[n] + r) + 5)

        @block.vector
        def _(dve):
            def split_lo(v, plus=0):
                if v >= 2 * N_UNITS:
                    return
                dve.wait_ge(w_hi_made, v + 1 + plus)
                nc.vector.tensor_tensor(w_lo[:, v % 4, :],
                                        raw[:, v // 2 % 4, (v % 2) * HALF:(v % 2 + 1) * HALF],
                                        w_hi[:, v % 4, :].bitcast(f32), ALU.subtract)\
                         .then_inc(raw_done, 1)

            def add_mod(m, tile, plus=0):
                chunk, k = m // KT, m - MODS_ALONE
                dve.wait_ge(acc_ready[chunk % 2], 16 * (chunk // 2))
                dve.wait_ge(mod_in[m % 2], 16 * (k // 2 + 1) + 8 * plus)
                dve.wait_ge(mod_done, k + 2 + plus)
                part = acc[:, chunk % 2, :]
                nc.vector.scalar_tensor_tensor(out=part, in0=mod_raw[:, m % 2, :],
                                               scalar=cT[:, ds(tile, 1)], in1=part,
                                               op0=ALU.mult, op1=ALU.add).then_inc(mod_done, 1)

            def modulate_lo(n, first, last):
                for k in range(first, last):
                    dve.wait_ge(hm_hi_made, n * KT + k + 1)
                    nc.vector.tensor_scalar(xnT[:, k, :], xnT[:, k, :], scale_p[:, k:k + 1],
                                            shift_p[:, k:k + 1], ALU.mult, ALU.add)\
                             .then_inc(hm_full, 1)
                    dve.wait_ge(hm_full, n * KT + k + 1)
                    nc.vector.tensor_tensor(hm_lo[:, k, :], xnT[:, k, :],
                                            hm_hi[:, k, :].bitcast(f32), ALU.subtract)\
                             .then_inc(hm_made, 1)

            for n in range(2):
                nc.vector.memset(acc[:, n, :], 0.0).then_inc(acc_cleared, 1)
            dve.wait_ge(params_made, 1)
            for n in range(2):
                dve.wait_ge(acc_first[n], 16)
                with dve.Fori(0, KT // 4) as i:
                    for r in range(4):
                        dve.wait_ge(raw_in[r], 16 * (n * KT // 4 + 1) + 16 * i)
                        dve.wait_ge(raw_done, 8 + 2 * (n * KT + r) + 8 * i)
                        nc.vector.scalar_tensor_tensor(out=acc[:, n, :], in0=raw[:, r, :],
                                                       scalar=cT[:, ds(4 * i + r, 1)],
                                                       in1=acc[:, n, :], op0=ALU.mult, op1=ALU.add)\
                                 .then_inc(raw_done, 2)
            dve.wait_ge(gb_in, 32)
            nc.vector.tensor_scalar(gate_b15, gate_b, 1.0 / GATE_CAP, None, ALU.mult)\
                     .then_inc(gb_scaled, 1)
            dve.wait_ge(sc_made, 2)
            for g in range(4):
                modulate_lo(0, 4 * g, 4 * g + 4)
                split_lo(g)
            with dve.Fori(0, 2) as i:
                for r in range(8):
                    split_lo(2 * (U_V + r) + 4, 16 * i)
                    add_mod(2 * KT + r, 8 * i + r, 8 * i)
                    split_lo(2 * (U_V + r) + 5, 16 * i)
            split_lo(2 * U_HEAD + 4)
            split_lo(2 * U_HEAD + 5)
            dve.wait_ge(lf_made, 1)
            dve.wait_ge(consts_made, 5)
            nc.vector.tensor_tensor_scan(neg_b[:], ones_row[:], neg_lf[:], 0.0, ALU.mult, ALU.add)\
                     .then_inc(b_made, 1)
            dve.wait_ge(b_made, 1)
            nc.vector.scalar_tensor_tensor(out=a_row[:], in0=th_i[:], scalar=GATE_CAP, in1=neg_b[:],
                                           op0=ALU.mult, op1=ALU.add).then_inc(a_made, 1)
            dve.wait_ge(a_made, 1)
            nc.vector.tensor_tensor_scan(m_row[:], a_row[:], a_row[:], 0.0, ALU.max, ALU.max)\
                     .then_inc(m_made, 1)
            dve.wait_ge(m_made, 1)
            nc.vector.tensor_tensor(neg_m[:], neg_b[:], m_row[:], ALU.subtract).then_inc(nm_made, 1)
            split_lo(2 * U_HEAD + 6)
            split_lo(2 * U_HEAD + 7)

            dve.wait_ge(aem_made, 1)

            def head(h, last):
                if last:
                    h, u, m, plus, mplus = H - 1, U_HEAD + 2 + 4 * (H - 1), 4 * KT - 2, 0, 0
                else:
                    u, m, plus, mplus = U_HEAD + 2, 3 * KT, 8 * h, 2 * h
                dve.wait_ge(scores_made, h + 1)
                nc.vector.tensor_scalar(m_sel[:], m_row[:], ident[0:H, ds(h, 1)], None, ALU.mult)\
                         .then_inc(m_sel_made, 1)
                split_lo(2 * u + 4, plus)
                add_mod(m, 2 * h, mplus)
                split_lo(2 * u + 5, plus)
                dve.wait_ge(scores_made, h + 2)
                nc.vector.scalar_tensor_tensor(out=weights[:, 0:SEQ], in0=ps[:, 0, 0:SEQ],
                                               scalar=a_em[:, 0, ds(h, 1)], in1=mask[:, 0:SEQ],
                                               op0=ALU.subtract, op1=ALU.max).then_inc(gaps_made, 1)
                nc.vector.scalar_tensor_tensor(out=weights[:, SEQ:SEQ + P], in0=ps[:, 0, P:SEQ],
                                               scalar=a_em[:, 1, ds(h, 1)], in1=mask[:, 0:P],
                                               op0=ALU.subtract, op1=ALU.max).then_inc(gaps_made, 1)
                dve.wait_ge(exp_made, h + 1)
                dve.wait_ge(pv_done, h + 1)
                nc.vector.scalar_tensor_tensor(out=probs[:], in0=ps[:, 1, 0:SEQ + P],
                                               scalar=float(DK) ** -0.5, in1=weights[:],
                                               op0=ALU.mult, op1=ALU.mult).then_inc(probs_made, 1)
                split_lo(2 * u + 6, plus)
                split_lo(2 * u + 7, plus)
                dve.wait_ge(pv_done, h + 2)
                den = ps[:, 2:4, DV]
                nc.vector.tensor_scalar(neg_den, den, -1.0, None, ALU.mult).then_inc(den_step, 1)
                dve.wait_ge(den_step, 3 * h + 1)
                nc.vector.tensor_tensor(den_abs, neg_den, den, ALU.max).then_inc(den_step, 1)
                dve.wait_ge(den_step, 3 * h + 2)
                nc.vector.tensor_tensor(den_max, den_abs,
                                        a_em[:, 2:4, ds(h, 1)].rearrange("p a o -> p (a o)"),
                                        ALU.max).then_inc(den_step, 1)
                dve.wait_ge(den_step, 3 * h + 3)
                nc.vector.reciprocal(rden, den_max).then_inc(rden_made, 1)
                if not last:
                    split_lo(2 * u + 8, plus)
                dve.wait_ge(h_rstd_made, h + 1)
                for t in range(TB):
                    nc.vector.tensor_scalar(h_tok[:, t, :], ps[:, 2 + t, 0:DV], rden[:, t:t + 1],
                                            h_rstd[:, t:t + 1], ALU.mult, ALU.mult)\
                             .then_inc(h_made, 1)
                if not last:
                    split_lo(2 * u + 9, plus)
                add_mod(m + 1, 2 * h + 1, mplus)
                if not last:
                    split_lo(2 * u + 10, plus)
                dve.wait_ge(hT_ready, h + 1)
                dve.wait_ge(sig_made, h + 1)
                dve.wait_ge(o_made, h + 1)
                for j in range(2):
                    nc.vector.scalar_tensor_tensor(out=gated[:, j * SEQ:(j + 1) * SEQ],
                                                   in0=ps[:, 0, j * SEQ:(j + 1) * SEQ],
                                                   scalar=hnT[:, ds(2 * h + j, 1)],
                                                   in1=o_sig[:, j * SEQ:(j + 1) * SEQ],
                                                   op0=ALU.mult, op1=ALU.mult).then_inc(gated_made, 1)
                if not last:
                    split_lo(2 * u + 11, plus)

            with dve.Fori(0, H - 1) as h:
                head(h, False)
            head(H - 1, True)

            def scale_y(yq, unit_end, gates, i=0, plus=0):
                dve.wait_ge(half_done, 2 * unit_end + 2 + plus)
                dve.wait_ge(a_free, gates)
                for t in range(TB):
                    dve.wait_ge(x_added, 2 * (yq + i) + t + 1)
                    nc.vector.tensor_tensor(y_tmp[:, t, :], ps[:, 2 * (yq % 2) + t, :],
                                            g_bc[:, ds((yq % 4 + i) * QUARTER, QUARTER)], ALU.mult)\
                             .then_inc(y_scaled, 1)

            with dve.Fori(0, 2) as i:
                for r in range(8):
                    split_lo(2 * (U_OUT + r) + 4, 16 * i)
                    add_mod(4 * KT + r, 8 * i + r, 8 * i)
                    if r % 4 == 3:
                        scale_y(Y_OUT + r // 4, U_OUT + r, 4, 2 * i, 16 * i)
                    split_lo(2 * (U_OUT + r) + 5, 16 * i)
            dve.wait_ge(sc_made, 4)
            modulate_lo(1, 0, KT)
            for n, tiles in enumerate(CHUNKS):
                with dve.Fori(0, tiles // 2) as i:
                    for r in range(4):
                        u, a, k = U_UP[n] + r, A_UP[n] + r, r // 2
                        pair = PAIR0[n] + k
                        done = 2 * pair + r % 2
                        buf = (conv_val if r % 2 else conv_gate)[:, k, :]
                        col = 2 * i + (FT if r % 2 else 0) + pair
                        split_lo(2 * u + 4, 8 * i)
                        if n == 0 and r % 2:
                            add_mod(5 * KT + k, 2 * i + k, 2 * i)
                        dve.wait_ge(conv_base, 4 * i + done + 1)
                        nc.vector.scalar_tensor_tensor(out=buf[:, 1:SEQ], in0=ps[:, 4 + r, 0:SEQ - 1],
                                                       scalar=cvT[:, ds(col + 2 * FT, 1)],
                                                       in1=buf[:, 1:SEQ], op0=ALU.mult, op1=ALU.add)\
                                 .then_inc(tap1_made, 1)
                        dve.wait_ge(tap1_made, 4 * i + done + 1)
                        nc.vector.scalar_tensor_tensor(out=buf[:, 2:SEQ], in0=ps[:, 4 + r, 0:SEQ - 2],
                                                       scalar=cvT[:, ds(col, 1)],
                                                       in1=buf[:, 2:SEQ], op0=ALU.mult, op1=ALU.add)\
                                 .then_inc(a_free, 1)
                        if r % 2:
                            dve.wait_ge(silu_made, 2 * i + pair + 1)
                            dve.wait_ge(a_free, 4 * i + 4 + a + 1)
                            nc.vector.tensor_tensor(act_hi[:, ds((2 * i + k) * SEQ, SEQ)],
                                                    conv_gate[:, k, :], conv_val[:, k, :], ALU.mult)\
                                     .then_inc(act_hi_made, 1)
                        split_lo(2 * u + 5, 8 * i)
                gates = 4 + A_G2 + 4
                if tiles == 16:
                    with dve.Fori(0, 2) as i:
                        for r in range(8):
                            split_lo(2 * (U_DOWN[n] + r) + 4, 16 * i)
                            if r % 4 == 3:
                                scale_y(Y_DOWN[n] + r // 4, U_DOWN[n] + r, gates, 2 * i, 16 * i)
                            split_lo(2 * (U_DOWN[n] + r) + 5, 16 * i)
                else:
                    g = tiles // 4
                    for r in range(tiles):
                        split_lo(2 * (U_DOWN[n] + r) + 4)
                        if r % g == g - 1:
                            scale_y(Y_DOWN[n] + r // g, U_DOWN[n] + r, gates)
                        split_lo(2 * (U_DOWN[n] + r) + 5)

        @block.tensor
        def _(pe):
            mm = nc.tensor.matmul

            def a_unit(u, a, plus=0, aplus=0, need=None):
                pe.wait_ge(a_free, a + 1 + aplus)
                out = ps[:, 4 + a % 4, 0:SEQ]
                for half in range(2):
                    v = 2 * u + half
                    pe.wait_ge(raw_done, RAW0 + v + 1 + plus)
                    if need is not None:
                        pe.wait_ge(hm_made, need + (half + 1) * KT // 2)
                    for j in range(KT // 2):
                        k = half * KT // 2 + j
                        hi = w_hi[:, v % 4, j * P:(j + 1) * P]
                        lo = w_lo[:, v % 4, j * P:(j + 1) * P]
                        mm(out, hi, hm_hi[:, k, :], start=(k == 0), stop=False)
                        mm(out, hi, hm_lo[:, k, :], start=False, stop=False)
                        last = mm(out, lo, hm_hi[:, k, :], start=False, stop=(k == KT - 1))
                    last.then_inc(half_done, 1)

            def b_unit(u, banks, group, groups, act_hi3, act_lo3, plus=0):
                for half in range(2):
                    v = 2 * u + half
                    pe.wait_ge(raw_done, RAW0 + v + 1 + plus)
                    for j in range(2):
                        k = 4 * group + 2 * half + j
                        first, final = k == 0, k == 4 * groups - 1
                        hi = w_hi[:, v % 4, j * QUARTER:(j + 1) * QUARTER]
                        lo = w_lo[:, v % 4, j * QUARTER:(j + 1) * QUARTER]
                        for t in range(TB):
                            out = ps[:, banks + t, :]
                            s_hi = act_hi3[:, k, t * P:(t + 1) * P]
                            s_lo = act_lo3[:, k, t * P:(t + 1) * P]
                            mm(out, s_hi, hi, start=first, stop=False)
                            mm(out, s_hi, lo, start=False, stop=False)
                            last = mm(out, s_lo, hi, start=False, stop=final)
                    last.then_inc(half_done, 1)

            def column_sums(n, bank):
                for k in range(KT):
                    last = mm(ps[:, bank, k:k + 1], acc[:, n % 2, k * P:(k + 1) * P], ones[:, 0:1],
                              start=True, stop=True)
                last.then_inc(colsum_done, 1)

            def gate_rows(n, g):
                for b in range(4):
                    last = mm(ps[:, 4 + b, :], ones[:], acc[:, n % 2, b * QUARTER:(b + 1) * QUARTER],
                              start=True, stop=True)
                    last.then_inc(g_summed, 1)
                pe.wait_ge(g_summed, 4 * g + 4)
                mm(ps[:, 3, 0:1], ones[:], ones[:, 0:1], start=True, stop=True).then_inc(colsum_done, 1)

            def transpose_x(n):
                pe.wait_ge(xn_made, TB * (n + 1))
                for g in range(KT // 2):
                    if n * KT // 2 + g >= 4:
                        pe.wait_ge(xT_copied, n * KT // 2 + g - 3)
                    for j in range(2):
                        for t in range(TB):
                            k = 2 * g + j
                            last = nc.tensor.transpose(
                                ps[:, 4 + g % 4, j * SEQ + t * P:j * SEQ + (t + 1) * P],
                                xn[:, t, k * P:(k + 1) * P], ident[:])
                    last.then_inc(xT_ready, 1)

            pe.wait_ge(consts_made, 4)
            pe.wait_ge(silu_c, 1)
            nc.tensor.transpose(ps[:, 0, 0:KT], c_rows[:], ident[0:KT, 0:KT]).then_inc(params_T, 1)
            pe.wait_ge(hn_in, 16)
            nc.tensor.transpose(ps[:, 1, 0:KT], hn_rows[:], ident[0:KT, 0:KT]).then_inc(params_T, 1)
            pe.wait_ge(cv_in, 32)
            for j in range(4):
                last = nc.tensor.transpose(ps[:, 2, j * 2 * FT:(j + 1) * 2 * FT], cv_rows[:, j, :],
                                           ident[0:2 * FT, 0:2 * FT])
            last.then_inc(params_T, 1)
            transpose_x(0)
            pe.wait_ge(params_made, 2)
            pe.wait_ge(raw_done, 8 + 2 * KT)
            column_sums(0, 0)
            pe.wait_ge(raw_done, 8 + 4 * KT)
            column_sums(1, 1)
            pe.wait_ge(sc_made, 2)
            pe.wait_ge(params_made, 3)
            with pe.Fori(0, 2) as i:
                for r in range(8):
                    if r % 4 == 0:
                        pe.wait_ge(v_copied, 4 * i + 2 * (r // 4) + 2)
                    pe.wait_ge(hm_made, 4 * (r % 4) + 4)
                    b_unit(U_V + r, 2 * (r // 4), r % 4, 4, hm_hi, hm_lo, 16 * i)
            pe.wait_ge(wg_made, 1)
            pe.wait_ge(v_copied, 4 + 6)
            for t in range(TB):
                for k in range(KT):
                    out = ps[:, 0, t * 2 * H:(t + 1) * 2 * H]
                    tok = slice(t * P, (t + 1) * P)
                    mm(out, hm_hi[:, k, tok], wg_hi[:, k, :], start=(k == 0), stop=False)
                    mm(out, hm_hi[:, k, tok], wg_lo[:, k, :], start=False, stop=False)
                    last = mm(out, hm_lo[:, k, tok], wg_hi[:, k, :], start=False, stop=(k == KT - 1))
            last.then_inc(g_ready, 1)
            pe.wait_ge(mod_done, 2 + KT)
            pe.wait_ge(xT_copied, KT // 2)
            pe.wait_ge(v_copied, 4 + 8)
            gate_rows(2, 0)
            a_unit(U_HEAD, A_HEAD)
            pe.wait_ge(g_copied, 1)
            for j in range(2):
                for t in range(TB):
                    last = mm(ps[0:H, 1, j * SEQ + t * P:j * SEQ + (t + 1) * P],
                              g_sb[:, t, j * H:(j + 1) * H], ident[:], start=True, stop=True)
            last.then_inc(g_rows, 1)
            a_unit(U_HEAD + 1, A_HEAD + 1)
            pe.wait_ge(em_made, 1)
            for j, row in ((0, a_row), (1, em_row)):
                for t in range(TB):
                    c0 = (2 * j + t) * H
                    last = mm(ps[:, 0, c0:c0 + H], row[:, t * P:(t + 1) * P], ident[0:H, 0:H],
                              start=True, stop=True)
            last.then_inc(aem_ready, 1)
            pe.wait_ge(aem_made, 1)

            def head(h, last_head):
                if last_head:
                    h, u, a, plus, aplus = H - 1, U_HEAD + 2 + 4 * (H - 1), A_HEAD + 2 + 4 * (H - 1), 0, 0
                else:
                    u, a, plus, aplus = U_HEAD + 2, A_HEAD + 2, 8 * h, 4 * h
                a_unit(u, a, plus, aplus)
                pe.wait_ge(m_sel_made, h + 1)
                pe.wait_ge(gated_made, 2 * h + 2)
                mm(ps[:, 0, 0:SEQ], ones[0:H, :], m_sel[:], start=True, stop=True)
                pe.wait_ge(probs_made, h + 1)
                pe.wait_ge(a_free, 4 * h + 6)
                mm(ps[:, 1, 0:SEQ], kT[:, 0:P], qT[:], start=True, stop=True)
                mm(ps[:, 1, SEQ:SEQ + P], kT[:, P:SEQ], qT[:, P:SEQ], start=True, stop=True)\
                    .then_inc(scores_made, 1)
                a_unit(u + 1, a + 1, plus, aplus)
                pe.wait_ge(probs_made, h + 2)
                pe.wait_ge(h_made, 2 * h + 2)
                vcol = ds(DV * h, DV)
                mm(ps[:, 2, 0:DV], probs[:, 0:P], v[:, 0, vcol], start=True, stop=True)
                mm(ps[:, 2, DV:DV + 1], probs[:, 0:P], ones[:, 0:1], start=True, stop=True)
                mm(ps[:, 3, 0:DV], probs[:, P:SEQ], v[:, 0, vcol], start=True, stop=False)
                mm(ps[:, 3, 0:DV], probs[:, SEQ:SEQ + P], v[:, 1, vcol], start=False, stop=True)
                mm(ps[:, 3, DV:DV + 1], probs[:, P:SEQ], ones[:, 0:1], start=True, stop=False)
                mm(ps[:, 3, DV:DV + 1], probs[:, SEQ:SEQ + P], ones[:, 0:1], start=False, stop=True)\
                    .then_inc(pv_done, 1)
                if last_head:
                    pe.wait_ge(mod_done, 2 + 2 * KT)
                    column_sums(3, 1)
                else:
                    a_unit(u + 2, a + 2, plus, aplus)
                pe.wait_ge(h_made, 2 * h + 4)
                for j in range(2):
                    for t in range(TB):
                        last = nc.tensor.transpose(ps[:, 0, j * SEQ + t * P:j * SEQ + (t + 1) * P],
                                                   h_tok[:, t, j * P:(j + 1) * P], ident[:])
                last.then_inc(hT_ready, 1)
                if not last_head:
                    a_unit(u + 3, a + 3, plus, aplus)

            with pe.Fori(0, H - 1) as h:
                head(h, False)
            head(H - 1, True)
            o_hi3 = o_hi[:].rearrange("p (k t) -> p k t", k=KT)
            o_lo3 = o_lo[:].rearrange("p (k t) -> p k t", k=KT)
            pe.wait_ge(o_made, H + 1)
            pe.wait_ge(sc_made, 3)
            with pe.Fori(0, 2) as i:
                for r in range(8):
                    if r % 4 == 0:
                        pe.wait_ge(y_scaled, 4 * i + 2 * (Y_OUT + r // 4) + 2)
                    b_unit(U_OUT + r, 2 * (r // 4), r % 4, 4, o_hi3, o_lo3, 16 * i)
            pe.wait_ge(y_scaled, 4 + 6)
            pe.wait_ge(mod_done, 2 + 3 * KT)
            column_sums(4, 0)
            transpose_x(1)
            act_hi3 = act_hi[:].rearrange("p (k t) -> p k t", k=16)
            act_lo3 = act_lo[:].rearrange("p (k t) -> p k t", k=16)
            pe.wait_ge(xT_copied, KT)
            pe.wait_ge(sc_made, 4)
            for n, tiles in enumerate(CHUNKS):
                with pe.Fori(0, tiles // 2) as i:
                    for r in range(4):
                        a_unit(U_UP[n] + r, A_UP[n] + r, 8 * i, 4 * i, need=KT)
                if n == 0:
                    pe.wait_ge(mod_done, 2 + 4 * KT)
                    pe.wait_ge(a_free, 4 + A_G2)
                    gate_rows(5, 1)
                groups = tiles // 4
                if tiles == 16:
                    with pe.Fori(0, 2) as i:
                        for r in range(8):
                            if r % 4 == 0:
                                pe.wait_ge(y_scaled, 4 * i + 2 * (Y_DOWN[n] + r // 4) + 2)
                            pe.wait_ge(pair_done, 2 + PAIR0[n] + 4 * (r % 4) + 4)
                            b_unit(U_DOWN[n] + r, 2 * (r // 4), r % 4, 4, act_hi3, act_lo3, 16 * i)
                else:
                    for r in range(tiles):
                        quarter, group = r // groups, r % groups
                        if group == 0:
                            pe.wait_ge(y_scaled, 2 * (Y_DOWN[n] + quarter) + 2)
                        pe.wait_ge(pair_done, 2 + PAIR0[n] + 4 * group + 4)
                        b_unit(U_DOWN[n] + r, 2 * (quarter % 2), group, groups, act_hi3, act_lo3)


_INS = ["x", "c", "l0_w_mod", "l0_b_mod", "l0_w_in", "l0_gate_bias", "l0_h_norm", "l0_w_out",
        "l0_w_up", "l0_conv_w", "l0_conv_b", "l0_w_down"]


def kernel(**inputs):
    import numpy as _np
    import concourse.bacc as _bacc
    from concourse import mybir as _mybir
    from concourse.bass_utils import run_bass_kernel_spmd as _run

    nc = _bacc.Bacc("TRN2", target_bir_lowering=False, num_devices=1)
    arrays, args = {}, []
    for name in _INS:
        a = _np.ascontiguousarray(inputs[name])
        arrays[f"in_{name}_dram"] = a
        args.append(nc.dram_tensor(f"in_{name}_dram", a.shape, _mybir.dt.from_np(a.dtype),
                                   kind="ExternalInput").ap())
    shape = inputs["x"].shape
    args.append(nc.dram_tensor("out_0_dram", shape, _mybir.dt.float32, kind="ExternalOutput").ap())
    hybrid_mlstm_convffn_adaln_kernel(nc, *args)
    r = _run(nc, [arrays], core_ids=[0])
    return r.results[0]["out_0_dram"]
```
